# Optimizing a Trainium2 kernel written in Bass

```python
import math
import jax, jax.numpy as jnp
from jax import lax
import numpy as np

D_MODEL = 1024
BATCH = 1
SEQ = 512
DEPTH = 1

PLE_DIM = 256
D_FF = 2816
POOL_WIDTH = 512
POOL_WINDOWS = (2, 4, 8, 16)
POOL_GROUPS = len(POOL_WINDOWS)
POOL_GROUP_DIM = POOL_WIDTH // POOL_GROUPS
HEAD_DIM = 64
N_Q_HEADS = 8
N_KV_HEADS = 2
Q_PER_KV = N_Q_HEADS // N_KV_HEADS
ATTN_WIDTH = N_Q_HEADS * HEAD_DIM
KV_WIDTH = N_KV_HEADS * HEAD_DIM
WINDOW = 128
BLOCK = 128
MIX_IN = POOL_WIDTH + ATTN_WIDTH + 2 * KV_WIDTH
MIX_OUT = POOL_WIDTH + ATTN_WIDTH
EPS = 1e-6
NEG_INF = -1e30

kernel_name = "hymba_pool_swa_sink_macaron_ple"

def rms_norm(x, g):
    xf = x.astype(jnp.float32)
    y = xf * lax.rsqrt(jnp.mean(xf * xf, axis=-1, keepdims=True) + EPS)
    return (y * g.astype(jnp.float32)).astype(x.dtype)

def swiglu(h, w_gate, w_up, w_down):
    return (jax.nn.silu(h @ w_gate) * (h @ w_up)) @ w_down

def causal_pool_mixer(u, pool_w, pool_scale):
    B, S, _ = u.shape
    ug_all = u.reshape(B, S, POOL_GROUPS, POOL_GROUP_DIM)
    pos = jnp.arange(S)
    outs = []
    for g, win in enumerate(POOL_WINDOWS):
        ug = ug_all[:, :, g, :].astype(jnp.float32)
        c = jnp.cumsum(ug, axis=1)
        c_shift = jnp.pad(c, ((0, 0), (win, 0), (0, 0)))[:, :S]
        count = jnp.minimum(pos + 1, win).astype(jnp.float32)[None, :, None]
        outs.append(((c - c_shift) / count - ug).astype(u.dtype))
    d = jnp.stack(outs, axis=2)
    y = jnp.einsum('bsgc,gcd->bsgd', d, pool_w).reshape(B, S, POOL_WIDTH)
    return y * pool_scale

def sliding_window_sink_attention(q, k, v, sinks):
    B, S, _, _ = q.shape
    nb = S // BLOCK
    qb = q.reshape(B, nb, BLOCK, N_KV_HEADS, Q_PER_KV, HEAD_DIM)
    kb = k.reshape(B, nb, BLOCK, N_KV_HEADS, HEAD_DIM)
    vb = v.reshape(B, nb, BLOCK, N_KV_HEADS, HEAD_DIM)
    pad = ((0, 0), (1, 0), (0, 0), (0, 0), (0, 0))
    k_band = jnp.concatenate([jnp.pad(kb, pad)[:, :nb], kb], axis=2)
    v_band = jnp.concatenate([jnp.pad(vb, pad)[:, :nb], vb], axis=2)
    scale = 1.0 / math.sqrt(HEAD_DIM)
    scores = jnp.einsum('bnqkgd,bnskd->bnkgqs', qb, k_band).astype(jnp.float32) * scale
    i = jnp.arange(BLOCK)[:, None]
    j = jnp.arange(2 * BLOCK)[None, :]
    rel = i + BLOCK - j
    band = (rel >= 0) & (rel < WINDOW)
    has_prev = (jnp.arange(nb)[:, None, None] > 0) | (j >= BLOCK)[None]
    mask = band[None] & has_prev
    scores = jnp.where(mask[None, :, None, None], scores, NEG_INF)
    s = sinks.astype(jnp.float32).reshape(N_KV_HEADS, Q_PER_KV)[None, None, :, :, None, None]
    m = jnp.maximum(jnp.max(scores, axis=-1, keepdims=True), s)
    e = jnp.exp(scores - m)
    probs = e / (jnp.sum(e, axis=-1, keepdims=True) + jnp.exp(s - m))
    out = jnp.einsum('bnkgqs,bnskd->bnqkgd', probs.astype(v.dtype), v_band)
    return out.reshape(B, S, ATTN_WIDTH)

def setup_inputs(seed: int = 0) -> dict:
    key = jax.random.key(seed)
    ks = jax.random.split(key, 24)
    f32 = jnp.float32

    def w(k, shape, fan_in):
        return jax.random.normal(k, shape, f32) * (fan_in ** -0.5)

    def gain(k, shape):
        return 1.0 + 0.05 * jax.random.normal(k, shape, f32)

    L = DEPTH
    return {
        "x": jax.random.normal(ks[0], (BATCH, SEQ, D_MODEL), f32),
        "p": jax.random.normal(ks[1], (DEPTH, BATCH, SEQ, PLE_DIM), f32),
        "ffn1_norm": gain(ks[2], (L, D_MODEL)),
        "ffn1_w_gate": w(ks[3], (L, D_MODEL, D_FF), D_MODEL),
        "ffn1_w_up": w(ks[4], (L, D_MODEL, D_FF), D_MODEL),
        "ffn1_w_down": w(ks[5], (L, D_FF, D_MODEL), D_FF),
        "mix_norm": gain(ks[6], (L, D_MODEL)),
        "w_in": w(ks[7], (L, D_MODEL, MIX_IN), D_MODEL),
        "pool_w": w(ks[8], (L, POOL_GROUPS, POOL_GROUP_DIM, POOL_GROUP_DIM), POOL_GROUP_DIM),
        "pool_scale": gain(ks[9], (L, POOL_WIDTH)),
        "q_norm": gain(ks[10], (L, HEAD_DIM)),
        "k_norm": gain(ks[11], (L, HEAD_DIM)),
        "attn_sinks": jax.random.normal(ks[12], (L, N_Q_HEADS), f32),
        "pool_out_norm": gain(ks[13], (L, POOL_WIDTH)),
        "attn_out_norm": gain(ks[14], (L, ATTN_WIDTH)),
        "w_out": w(ks[15], (L, MIX_OUT, D_MODEL), MIX_OUT),
        "ffn2_norm": gain(ks[16], (L, D_MODEL)),
        "ffn2_w_gate": w(ks[17], (L, D_MODEL, D_FF), D_MODEL),
        "ffn2_w_up": w(ks[18], (L, D_MODEL, D_FF), D_MODEL),
        "ffn2_w_down": w(ks[19], (L, D_FF, D_MODEL), D_FF),
        "ple_norm": gain(ks[20], (L, D_MODEL)),
        "w_ple_gate": w(ks[21], (L, D_MODEL, D_MODEL), D_MODEL),
        "w_ple_proj": w(ks[22], (L, PLE_DIM, D_MODEL), PLE_DIM),
    }

def reference(x, p, ffn1_norm, ffn1_w_gate, ffn1_w_up, ffn1_w_down, mix_norm, w_in,
              pool_w, pool_scale, q_norm, k_norm, attn_sinks, pool_out_norm, attn_out_norm,
              w_out, ffn2_norm, ffn2_w_gate, ffn2_w_up, ffn2_w_down, ple_norm,
              w_ple_gate, w_ple_proj):
    B, S, _ = x.shape
    o_q = POOL_WIDTH
    o_k = o_q + ATTN_WIDTH
    o_v = o_k + KV_WIDTH
    for i in range(DEPTH):
        h = rms_norm(x, ffn1_norm[i])
        x = x + 0.5 * swiglu(h, ffn1_w_gate[i], ffn1_w_up[i], ffn1_w_down[i])

        h = rms_norm(x, mix_norm[i])
        z = h @ w_in[i]
        u = z[..., :o_q]
        q = z[..., o_q:o_k].reshape(B, S, N_Q_HEADS, HEAD_DIM)
        k = z[..., o_k:o_v].reshape(B, S, N_KV_HEADS, HEAD_DIM)
        v = z[..., o_v:].reshape(B, S, N_KV_HEADS, HEAD_DIM)

        pool_y = causal_pool_mixer(u, pool_w[i], pool_scale[i])
        q = rms_norm(q, q_norm[i])
        k = rms_norm(k, k_norm[i])
        attn_y = sliding_window_sink_attention(q, k, v, attn_sinks[i])

        merged = jnp.concatenate([rms_norm(pool_y, pool_out_norm[i]),
                                  rms_norm(attn_y, attn_out_norm[i])], axis=-1)
        x = x + merged @ w_out[i]

        h = rms_norm(x, ffn2_norm[i])
        x = x + 0.5 * swiglu(h, ffn2_w_gate[i], ffn2_w_up[i], ffn2_w_down[i])

        gate = jax.nn.sigmoid(rms_norm(x, ple_norm[i]) @ w_ple_gate[i])
        x = x + gate * (p[i] @ w_ple_proj[i])
    return x


_drawn_inputs = setup_inputs


def setup_inputs(seed=0):
    import zlib

    import numpy as np

    out = dict(_drawn_inputs(seed))
    spreads = {}
    factors = {'attn_sinks': 6.033, 'ffn2_norm': 4.132, 'ple_norm': 8.0}
    for name, (base, spread) in spreads.items():
        noise = np.random.default_rng([zlib.crc32(name.encode()), seed]).standard_normal(out[name].shape)
        drawn = base * np.exp(spread * noise) if base else spread * noise
        out[name] = __import__('jax').numpy.asarray(drawn.astype(out[name].dtype))
    for name, factor in factors.items():
        out[name] = (out[name] * factor).astype(out[name].dtype)
    return out
```

```python
from contextlib import ExitStack

import concourse.bass as bass
from concourse import mybir

F32 = mybir.dt.float32
F32R = mybir.dt.float32r
ALU = mybir.AluOpType
ACT = mybir.ActivationFunctionType

P = 128
EPS = 1e-6
NEG = -1e30
POOL_WINDOWS = (2, 4, 8, 16)
SLOTS = 4
CHUNK = 1024


def layer(nc, x, p, ffn1_norm, ffn1_w_gate, ffn1_w_up, ffn1_w_down, mix_norm, w_in, pool_w, pool_scale,
          q_norm, k_norm, attn_sinks, pool_out_norm, attn_out_norm, w_out, ffn2_norm, ffn2_w_gate,
          ffn2_w_up, ffn2_w_down, ple_norm, w_ple_gate, w_ple_proj, out):
    _, S, D = x.shape
    FF = ffn1_w_gate.shape[2]
    HD = q_norm.shape[1]
    NQ = attn_sinks.shape[1]
    KD = D // P
    NB = S // P
    NF = FF // P
    G = len(POOL_WINDOWS)
    QP = NQ // 2
    PAD = max(POOL_WINDOWS)
    HALF = KD // 2
    GAINS = 4 * KD + 2 * G + QP + 2

    GU = 2 * NF
    DH = NF // 2
    FFN = GU + 2 * DH
    FFN1 = 0
    MIX = FFN1 + FFN
    C_K, C_Q, C_V, C_Q3 = MIX, MIX + 1, MIX + 4, MIX + 5
    C_U = MIX + 6
    C_POOLW = C_U + G
    C_WP = C_POOLW + 1
    C_WA = C_WP + HALF
    FFN2 = C_WA + HALF
    PROJ = FFN2 + FFN
    PLE = PROJ + 2
    CHUNKS = PLE + KD
    TWO_PART = {C_Q, C_Q + 1, C_Q + 2, C_Q3} | {C_WA + i for i in range(HALF)}
    QUADS = NF // 2

    def loads_of(slot, c0, quad=0):
        extra = sum(1 for c in TWO_PART if c <= c0 and c % SLOTS == slot)
        return 16 * (c0 // SLOTS + 1 + extra) + 16 * quad

    es = ExitStack()
    with es:
        def sb(name, shape, dt=F32, stack=es):
            return stack.enter_context(nc.sbuf_tensor(name, shape, dt))

        def sem(name):
            return es.enter_context(nc.semaphore(name))

        x_t = sb("x_t", [P, KD, S])
        h_hi = sb("h_hi", [P, KD, S], F32R)
        h_lo = sb("h_lo", [P, KD, S], F32R)
        raw = sb("raw", [P, SLOTS, CHUNK])
        w_hi = sb("w_hi", [P, SLOTS, CHUNK], F32R)
        w_lo = sb("w_lo", [P, SLOTS, CHUNK], F32R)
        rstd = sb("rstd", [P, S])
        sumsq = sb("sumsq", [P, S])
        tmp = sb("tmp", [P, 4, S])
        pt_hi = sb("pt_hi", [P, 2, S], F32R)
        pt_lo = sb("pt_lo", [P, 2, S], F32R)
        ident = sb("ident", [P, P])
        ones = sb("ones", [P, P])
        head_ones = sb("head_ones", [P, P])
        mask = sb("mask", [P, 2, P])
        inv_count = sb("inv_count", [P, PAD])
        gain = sb("gain", [P, GAINS])
        gain_qk = sb("gain_qk", [P, 1])
        gain_pool = sb("gain_pool", [P, G])
        sink_in = sb("sink_in", [P, NQ])
        sink = sb("sink", [P, NQ])
        eps = sb("eps", [P, 1])
        small = sb("small", [P, 2, 8, NQ])
        with ExitStack() as phase:
            x_nat = sb("x_nat", [P, NB, D], stack=phase)
            p_nat = sb("p_nat", [P, NB, 2 * P], stack=phase)
            gain_nat = sb("gain_nat", [GAINS, P], stack=phase)
        with ExitStack() as phase:
            act_hi = sb("act_hi", [P, NF, S], F32R, stack=phase)
            act_lo = sb("act_lo", [P, NF, S], F32R, stack=phase)
        with ExitStack() as phase:
            q_hi = sb("q_hi", [P, QP, S], F32R, stack=phase)
            q_lo = sb("q_lo", [P, QP, S], F32R, stack=phase)
            kz_hi = sb("kz_hi", [P, 2, S], F32R, stack=phase)
            kz_lo = sb("kz_lo", [P, 2, S], F32R, stack=phase)
            v_hi = sb("v_hi", [P, NB, P], F32R, stack=phase)
            v_lo = sb("v_lo", [P, NB, P], F32R, stack=phase)
            head_rstd = sb("head_rstd", [P, 2, S], stack=phase)
            win = sb("win", [P, 3, PAD + S], stack=phase)
            d_hi = sb("d_hi", [P, G, S], F32R, stack=phase)
            d_lo = sb("d_lo", [P, G, S], F32R, stack=phase)
            probs = sb("probs", [P, 2, NQ, 2 * P], stack=phase)
            pr_hi = sb("pr_hi", [P, 4, S], F32R, stack=phase)
            pr_lo = sb("pr_lo", [P, 4, S], F32R, stack=phase)
        with ExitStack() as phase:
            proj = sb("proj", [P, NB, D], stack=phase)
            gate = sb("gate", [P, NB, P * HALF], stack=phase)
            rstd_nat = sb("rstd_nat", [P, NB], stack=phase)
        probs_flat = probs[:].rearrange("p a n k -> p (a n k)")
        qk = [probs_flat[:, i * S:(i + 1) * S] for i in range(1 + QP)]
        qk_sq = [probs_flat[:, (5 + i) * S:(6 + i) * S] for i in range(3)]

        bank = [es.enter_context(nc.psum_tensor(f"bank{i}", [P, S], F32)) for i in range(8)]

        x_loaded = [sem(f"x_loaded{i}") for i in range(4)]
        p_loaded, gains_loaded, sinks_loaded = sem("p_loaded"), sem("gains_loaded"), sem("sinks_loaded")
        raw_loaded = [sem(f"raw_loaded{i}") for i in range(SLOTS)]
        w_hi_done, w_ready, w_used = sem("w_hi_done"), sem("w_ready"), sem("w_used")
        pool_consts, ident_ready, dve_consts = sem("pool_consts"), sem("ident_ready"), sem("dve_consts")
        gain1_loaded, gain_turned, gain1_ready, gain_ready = (
            sem("gain1_loaded"), sem("gain_turned"), sem("gain1_ready"), sem("gain_ready"))
        x_turned = sem("x_turned")
        p_turned, p_hi_done, p_ready = sem("p_turned"), sem("p_hi_done"), sem("p_ready")
        x_ready, h_hi_done, h_ready = sem("x_ready"), sem("h_hi_done"), sem("h_ready")
        sq_done, sumsq_added, stat_done, ln_done, rstd_ready = (
            sem("sq_done"), sem("sumsq_added"), sem("stat_done"), sem("ln_done"), sem("rstd_ready"))
        gate_scaled, silu_done, act_made, act_hi_done, act_ready = (
            sem("gate_scaled"), sem("silu_done"), sem("act_made"), sem("act_hi_done"), sem("act_ready"))
        down_done = sem("down_done")
        qk_scaled, qk_sq_done, head_ms_done, head_ln_done, head_rstd_ready = (
            sem("qk_scaled"), sem("qk_sq_done"), sem("head_ms_done"), sem("head_ln_done"), sem("head_rstd_ready"))
        qk_normed, qk_hi_done, qk_ready, kz_zeroed = (
            sem("qk_normed"), sem("qk_hi_done"), sem("qk_ready"), sem("kz_zeroed"))
        v_scaled, v_turned, v_hi_done, v_ready = sem("v_scaled"), sem("v_turned"), sem("v_hi_done"), sem("v_ready")
        u_scaled, win_step, win_summed = sem("u_scaled"), sem("win_step"), sem("win_summed")
        d_made, d_hi_done, d_ready = sem("d_made"), sem("d_hi_done"), sem("d_ready")
        pool_done, pool_hi_done, pool_sq_done, pool_ready, pool_summed = (
            sem("pool_done"), sem("pool_hi_done"), sem("pool_sq_done"), sem("pool_ready"), sem("pool_summed"))
        pool_stat, pool_ln, pool_rstd = sem("pool_stat"), sem("pool_ln"), sem("pool_rstd")
        s_done, s_taken, max_ready, exp_done, p_normed = (
            sem("s_done"), sem("s_taken"), sem("max_ready"), sem("exp_done"), sem("p_normed"))
        pr_turned, pr_hi_done, pr_ready = sem("pr_turned"), sem("pr_hi_done"), sem("pr_ready")
        pv_done, y_made, y_hi_done, y_sq_done, y_ready, y_summed = (
            sem("pv_done"), sem("y_made"), sem("y_hi_done"), sem("y_sq_done"), sem("y_ready"), sem("y_summed"))
        y_stat, y_ln, y_rstd = sem("y_stat"), sem("y_ln"), sem("y_rstd")
        wp_even, wp_added, wa_even = sem("wp_even"), sem("wp_added"), sem("wa_even")
        proj_even, proj_kept = sem("proj_done"), sem("proj_kept")
        ple_stat, ple_ln, ple_rstd = sem("ple_stat"), sem("ple_ln"), sem("ple_rstd")
        x_back, gate_tok, gate_ready, out_ready, out_stored = (
            sem("x_back"), sem("gate_tok"), sem("gate_ready"), sem("out_ready"), sem("out_stored"))
        dve_chain = sem("dve_chain")

        block = es.enter_context(nc.Block())

        def f32(ap):
            return ap.bitcast(F32)

        def halves(n):
            return ([4, 5, 6, 7], [0, 1, 2, 3]) if n == 0 else ([0, 1, 2, 3], [4, 5, 6, 7])

        def down_steps(eng, first, step):
            step(0, first % SLOTS, None)
            loops = (DH - 3) // SLOTS
            with eng.Fori(0, loops) as quad:
                for j in range(SLOTS):
                    step(1 + j, (first + 1 + j) % SLOTS, quad)
            for ch in range(1 + SLOTS * loops, DH):
                step(ch, (first + ch) % SLOTS, None)

        @block.sync
        def _(sp):
            def put(c, slot, parts, quad=0):
                if c >= SLOTS:
                    sp.wait_ge(w_ready, c - SLOTS + 1 + SLOTS * quad)
                for dst, src in parts:
                    sp.dma_start(dst, src).then_inc(raw_loaded[slot], 16)

            def ring(slot, cols, a):
                return raw[:, slot, 0:cols].rearrange("p (k c) -> p k c", k=a)

            def gate_up(c, slot, w, f, quad=0):
                put(c, slot, [(ring(slot, CHUNK, KD),
                               w[0].rearrange("(k p) c -> p k c", p=P)[:, :, bass.ts(f, P)])], quad)

            def load_ffn(c0, w_gate, w_up, w_down, first_quad):
                for j in range(0 if first_quad else SLOTS, SLOTS):
                    gate_up(c0 + j, (c0 + j) % SLOTS, (w_gate, w_up)[j % 2], j // 2)
                with sp.Fori(1, QUADS) as quad:
                    for j in range(SLOTS):
                        gate_up(c0 + j, (c0 + j) % SLOTS, (w_gate, w_up)[j % 2], quad * 2 + j // 2,
                                quad) if c0 + j >= SLOTS else first_ring(c0 + j, (w_gate, w_up)[j % 2], quad, j)
                wd = w_down[0].rearrange("(k p) c -> p k c", p=P)
                for half in range(2):
                    first = c0 + GU + half * DH

                    def step(ch, slot, quad):
                        q = 0 if quad is None else quad
                        put(first + ch, slot, [(ring(slot, CHUNK, 2),
                                                wd[:, bass.ds((q * SLOTS + ch) * 2, 2),
                                                   half * HALF * P:(half + 1) * HALF * P])], q)

                    down_steps(sp, first, step)

            def first_ring(c, w, quad, j):
                sp.wait_ge(w_ready, (quad - 1) * SLOTS + c + 1)
                sp.dma_start(ring(c, CHUNK, KD), w[0].rearrange("(k p) c -> p k c", p=P)[
                    :, :, bass.ts(quad * 2 + j // 2, P)]).then_inc(raw_loaded[c], 16)

            x_v = x[0].rearrange("(b p) c -> p b c", p=P)
            W = D // 4

            def load_x(i):
                sp.dma_start(x_nat[:, :, i * W:(i + 1) * W], x_v[:, :, i * W:(i + 1) * W]).then_inc(x_loaded[i], 16)

            load_x(0)
            gate_up(0, 0, ffn1_w_gate, 0)
            load_x(1)
            gate_up(1, 1, ffn1_w_up, 0)
            load_x(2)
            load_x(3)
            gate_up(2, 2, ffn1_w_gate, 1)
            gate_up(3, 3, ffn1_w_up, 1)
            sp.dma_start(p_nat[:], p[0, 0].rearrange("(b p) c -> p b c", p=P)).then_inc(p_loaded, 16)
            rows = KD
            for norm in (mix_norm, ffn2_norm, ple_norm, pool_scale, pool_out_norm):
                n = norm.shape[1] // P
                sp.dma_start(gain_nat[rows:rows + n, :], norm[0].rearrange("(k p) -> k p", p=P)).then_inc(gains_loaded, 16)
                rows += n
            for g in range(2):
                sp.dma_start(gain_nat[rows:rows + QP, g * HD:(g + 1) * HD],
                             attn_out_norm[0, g * QP * HD:(g + 1) * QP * HD].rearrange("(t c) -> t c", c=HD))\
                    .then_inc(gains_loaded, 16)
                sp.dma_start(gain_nat[rows + QP:rows + QP + 1, g * HD:(g + 1) * HD], q_norm).then_inc(gains_loaded, 16)
                sp.dma_start(gain_nat[rows + QP + 1:rows + QP + 2, g * HD:(g + 1) * HD], k_norm)\
                    .then_inc(gains_loaded, 16)
            sp.dma_start(sink_in[:], attn_sinks[0].partition_broadcast(P)).then_inc(sinks_loaded, 16)
            load_ffn(FFN1, ffn1_w_gate, ffn1_w_up, ffn1_w_down, False)

            w_in_v = w_in[0].rearrange("(k p) c -> p k c", p=P)
            o_q = G * P
            o_k = o_q + NQ * HD
            o_v = o_k + 2 * HD

            def load_in(c, col):
                put(c, c % SLOTS, [(ring(c % SLOTS, CHUNK, KD), w_in_v[:, :, col:col + P])])

            def load_q(c, t):
                put(c, c % SLOTS, [(ring(c % SLOTS, CHUNK, KD)[:, :, g * HD:(g + 1) * HD],
                                    w_in_v[:, :, o_q + (g * QP + t) * HD:o_q + (g * QP + t + 1) * HD])
                                   for g in range(2)])

            load_in(C_K, o_k)
            for t in range(3):
                load_q(C_Q + t, t)
            load_in(C_V, o_v)
            load_q(C_Q3, 3)
            for g in range(G):
                load_in(C_U + g, g * P)
            put(C_POOLW, C_POOLW % SLOTS, [(ring(C_POOLW % SLOTS, G * P, G), pool_w[0].rearrange("g c d -> c g d"))])
            for i in range(HALF):
                c = C_WP + i
                put(c, c % SLOTS, [(ring(c % SLOTS, CHUNK, G),
                                    w_out[0][0:G * P, i * 2 * P:(i + 1) * 2 * P].rearrange("(k p) c -> p k c", p=P))])
            for i in range(HALF):
                c = C_WA + i
                put(c, c % SLOTS, [
                    (ring(c % SLOTS, CHUNK, QP)[g * HD:(g + 1) * HD],
                     w_out[0][G * P + g * QP * HD:G * P + (g + 1) * QP * HD, i * 2 * P:(i + 1) * 2 * P]
                     .rearrange("(t p) c -> p t c", p=HD)) for g in range(2)])
            load_ffn(FFN2, ffn2_w_gate, ffn2_w_up, ffn2_w_down, True)
            for half in range(2):
                c = PROJ + half
                put(c, c % SLOTS, [(ring(c % SLOTS, CHUNK, 2), w_ple_proj[0].rearrange("(k p) c -> p k c", p=P)
                                    [:, :, half * S:(half + 1) * S])])
            for half in range(2):
                for i in range(HALF):
                    c = PLE + half * HALF + i
                    put(c, c % SLOTS, [(ring(c % SLOTS, CHUNK, 2), w_ple_gate[0].rearrange("(k p) c -> p k c", p=P)
                                        [:, 2 * i:2 * i + 2, half * S:(half + 1) * S])])
            for half in range(2):
                for b in range(NB):
                    sp.wait_ge(out_ready, half * NB + b + 1)
                    sp.dma_start(out[0, b * P:(b + 1) * P, half * S:(half + 1) * S],
                                 proj[:, b, half * S:(half + 1) * S]).then_inc(out_stored, 16)
            sp.wait_ge(out_stored, 16 * 2 * NB)

        @block.gpsimd
        def _(pool):
            pool.memset(ident[:], 0.0).then_inc(pool_consts, 1)
            pool.wait_ge(pool_consts, 1)
            pool.affine_select(out=ident[:], in_=ident[:], compare_op=ALU.not_equal, fill=1.0, base=0,
                               pattern=[[-1, P]], channel_multiplier=1).then_inc(ident_ready, 1)

            def lo_of(slot, count):
                pool.wait_ge(w_hi_done, count)
                pool.tensor_tensor(w_lo[:, slot, :], raw[:, slot, :], f32(w_hi[:, slot, :]),
                                   ALU.subtract).then_inc(w_ready, 1)

            for c in range(SLOTS):
                lo_of(c, c + 1)
            pool.memset(mask[:], 0.0).then_inc(pool_consts, 1)
            pool.wait_ge(pool_consts, 2)
            pool.affine_select(out=mask[:, 0, :], in_=mask[:, 0, :], compare_op=ALU.is_gt, fill=NEG, base=0,
                               pattern=[[1, P]], channel_multiplier=-1).then_inc(pool_consts, 1)
            pool.affine_select(out=mask[:, 1, :], in_=mask[:, 1, :], compare_op=ALU.is_ge, fill=NEG, base=0,
                               pattern=[[-1, P]], channel_multiplier=1).then_inc(pool_consts, 1)
            with pool.Fori(1, C_POOLW // SLOTS) as quad:
                for slot in range(SLOTS):
                    lo_of(slot, quad * SLOTS + slot + 1)
            steps = 0
            for g, w in enumerate(POOL_WINDOWS):
                lo_of(g, C_POOLW + g + 1)
                pool.wait_ge(u_scaled, g + 1)
                s, i = 1, 0
                while s < w:
                    src = win[:, 0 if i == 0 else 2 - i % 2, :]
                    dst = win[:, 1 + i % 2, :]
                    ins = pool.tensor_tensor(dst[:, PAD:], src[:, PAD:], src[:, PAD - s:PAD + S - s], ALU.add)
                    s, i = 2 * s, i + 1
                    if s < w:
                        steps += 1
                        ins.then_inc(win_step, 1)
                        pool.wait_ge(win_step, steps)
                ins.then_inc(win_summed, 1)
            with pool.Fori(C_POOLW // SLOTS + 1, CHUNKS // SLOTS) as quad:
                for slot in range(SLOTS):
                    lo_of(slot, quad * SLOTS + slot + 1)
            for c in range(CHUNKS // SLOTS * SLOTS, CHUNKS):
                lo_of(c % SLOTS, c + 1)

        @block.scalar
        def _(act):
            def split(c, slot=None, quad=0):
                slot = c % SLOTS if slot is None else slot
                act.wait_ge(raw_loaded[slot], loads_of(slot, c, quad))
                if c >= SLOTS:
                    act.wait_ge(w_used, c - SLOTS + 1 + SLOTS * quad)
                nc.scalar.activation(w_hi[:, slot, :], raw[:, slot, :], ACT.Copy).then_inc(w_hi_done, 1)

            def h_round(ph, d):
                act.wait_ge(x_ready, ph * KD + d + 1)
                if ph == 2 and d == HALF:
                    act.wait_ge(w_used, C_WA + HALF)
                if ph == 2 and d == 0:
                    act.wait_ge(w_used, C_WP + HALF)
                nc.scalar.activation(h_hi[:, d, :], x_t[:, d, :], ACT.Copy,
                                     scale=gain[:, ph * KD + d:ph * KD + d + 1]).then_inc(h_hi_done, 1)

            def h_square(ph, d):
                act.wait_ge(x_ready, ph * KD + d + 1)
                if d == 0:
                    if ph == 2:
                        act.wait_ge(pool_stat, 1)
                    nc.scalar.activation(sumsq[:], x_t[:, 0, :], ACT.Square).then_inc(sq_done, 1)
                    return
                if d >= 3:
                    act.wait_ge(sumsq_added, ph * (KD - 1) + d - 2)
                nc.scalar.activation(tmp[:, 2 + d % 2, :], x_t[:, d, :], ACT.Square).then_inc(sq_done, 1)

            def rsqrt(dst, src, n, ln_sem, ln_count, out_sem):
                nc.scalar.activation(dst, src, ACT.Ln, scale=1.0 / n, bias=eps[:, 0:1]).then_inc(ln_sem, 1)
                act.wait_ge(ln_sem, ln_count)
                nc.scalar.activation(dst, dst, ACT.Exp, scale=-0.5).then_inc(out_sem, 1)

            def rstd_of(ph, b):
                act.wait_ge(stat_done, ph + 1)
                rsqrt(rstd[:], bank[b][:], D, ln_done, ph + 1, rstd_ready)

            def swiglu(n, f, quad=0):
                count = n * NF + f + 1 + 2 * quad
                act.wait_ge(gate_scaled, count)
                nc.scalar.activation(tmp[:, 2 * (f % 2), :], tmp[:, 2 * (f % 2), :], ACT.Silu).then_inc(silu_done, 1)
                act.wait_ge(act_made, count)
                nc.scalar.activation(act_hi[:, f + 2 * quad, :], tmp[:, 2 * (f % 2) + 1, :],
                                     ACT.Copy).then_inc(act_hi_done, 1)

            def ffn_scalar(n, c0):
                with act.Fori(1, QUADS) as quad:
                    for j in range(SLOTS):
                        slot = (c0 + j) % SLOTS
                        act.wait_ge(raw_loaded[slot], loads_of(slot, c0 + j, quad))
                        act.wait_ge(w_used, (quad - 1) * SLOTS + c0 + j + 1)
                        nc.scalar.activation(w_hi[:, slot, :], raw[:, slot, :], ACT.Copy).then_inc(w_hi_done, 1)
                        if j in (1, 3):
                            swiglu(n, j // 2, quad - 1)
                for j in range(SLOTS):
                    split(c0 + GU + j)
                    if j in (1, 3):
                        swiglu(n, NF - 2 + j // 2)
                for half in range(2):
                    first = c0 + GU + SLOTS + half * DH
                    if half == 0:
                        down_steps(act, first, lambda ch, slot, quad: split(
                            first + ch, slot, 0 if quad is None else quad))
                        for d in range(HALF):
                            h_round(n * 2 + 1, d)
                            h_square(n * 2 + 1, d)
                    elif n == 0:
                        for ch in range(DH):
                            split(first + ch)
                    else:
                        down_steps(act, first, lambda ch, slot, quad: split(
                            first + ch, slot, 0 if quad is None else quad))
                for d in range(HALF, KD):
                    h_round(n * 2 + 1, d)

            act.dma_start(gain_nat[0:KD, :], ffn1_norm[0].rearrange("(k p) -> k p", p=P)).then_inc(gain1_loaded, 16)
            act.preload_act_table_set("natural_log_exp_and_others")
            split(0)
            act.wait_ge(gain1_ready, 1)
            h_round(0, 0)
            h_round(0, 1)
            split(1)
            h_square(0, 0)
            h_square(0, 1)
            h_round(0, 2)
            h_round(0, 3)
            h_square(0, 2)
            h_square(0, 3)
            h_round(0, 4)
            h_round(0, 5)
            split(2)
            h_round(0, 6)
            h_round(0, 7)
            split(3)
            for d in range(HALF, KD):
                h_square(0, d)
            for k in range(2):
                act.wait_ge(p_turned, k + 1)
                nc.scalar.activation(pt_hi[:, k, :], bank[5 + k][:], ACT.Copy).then_inc(p_hi_done, 1)
            rstd_of(0, 4)
            ffn_scalar(0, FFN1)
            for d in range(HALF, KD):
                h_square(1, d)

            act.preload_act_table_set("natural_log_exp_and_others")
            split(C_V)
            rstd_of(1, 0)
            split(C_Q3)

            def qk_square(i):
                act.wait_ge(qk_scaled, i + 1)
                if i >= 3:
                    act.wait_ge(head_ms_done, i - 2)
                nc.scalar.activation(qk_sq[i % 3], qk[i], ACT.Square).then_inc(qk_sq_done, 1)

            def head_rsqrt(i):
                act.wait_ge(head_ms_done, i + 1)
                if i >= 2:
                    act.wait_ge(qk_normed, i - 1)
                rsqrt(head_rstd[:, i % 2, :], bank[(0, 3)[i % 2]][:], HD, head_ln_done, i + 1, head_rstd_ready)

            def qk_round(i):
                act.wait_ge(qk_normed, i + 1)
                if i == 0:
                    act.wait_ge(kz_zeroed, 4)
                    for g in range(2):
                        rows = slice(g * HD, (g + 1) * HD)
                        nc.scalar.activation(kz_hi[rows, g, :], qk[0][rows], ACT.Copy).then_inc(qk_hi_done, 1)
                else:
                    nc.scalar.activation(q_hi[:, i - 1, :], qk[i], ACT.Copy).then_inc(qk_hi_done, 1)

            def d_round(g):
                act.wait_ge(d_made, g + 1)
                nc.scalar.activation(d_hi[:, g, :], head_rstd[:, 1, :], ACT.Copy).then_inc(d_hi_done, 1)

            def softmax(b):
                act.wait_ge(max_ready, b + 1)
                nc.scalar.activation(small[:, b % 2, 3, :], small[:, b % 2, 2, :], ACT.Exp).then_inc(exp_done, 1)
                lo = P if b == 0 else 0
                for n in range(NQ):
                    nc.scalar.activation(probs[:, b % 2, n, lo:], probs[:, b % 2, n, lo:], ACT.Exp,
                                         bias=small[:, b % 2, 1, n:n + 1],
                                         accum_out=small[:, b % 2, 4, n:n + 1]).then_inc(exp_done, 1)

            def pr_round(b):
                for i, slot in enumerate((1, 3) if b == 0 else range(4)):
                    act.wait_ge(pr_turned, (0 if b == 0 else 4 * b - 2) + i + 1)
                    nc.scalar.activation(pr_hi[:, slot, :], bank[slot][:], ACT.Copy).then_inc(pr_hi_done, 1)

            def y_round(b):
                for g in range(2):
                    rows = slice(g * HD, (g + 1) * HD)
                    act.wait_ge(y_made, 2 * b + g + 1)
                    if b:
                        act.wait_ge(y_summed, b)
                    nc.scalar.activation(tmp[rows, 2, :], bank[4 + g][rows], ACT.Square).then_inc(y_sq_done, 1)
                act.wait_ge(y_made, 2 * b + 2)
                nc.scalar.activation(h_hi[:, G:, b * P:(b + 1) * P], tmp[:, 1, :].rearrange("p (t q) -> p t q", t=QP),
                                     ACT.Copy).then_inc(y_hi_done, 1)

            def pool_round(g):
                act.wait_ge(pool_done, g + 1) if g < G - 1 else act.wait_ge(w_used, C_POOLW + 1)
                src = bank[6 + g % 2][:]
                nc.scalar.activation(h_hi[:, g, :], src, ACT.Copy, scale=gain_pool[:, g:g + 1]).then_inc(pool_hi_done, 1)
                if g == 0:
                    act.wait_ge(u_scaled, G)
                if g > 1:
                    act.wait_ge(pool_summed, g - 1)
                nc.scalar.activation(sumsq[:] if g == 0 else rstd[:], src, ACT.Square,
                                     scale=gain[:, 4 * KD + g:4 * KD + g + 1]).then_inc(pool_sq_done, 1)

            qk_square(0)
            split(C_U)
            qk_square(1)
            split(C_U + 1)
            qk_square(2)
            head_rsqrt(0)
            qk_round(0)
            qk_square(3)
            head_rsqrt(1)
            qk_round(1)
            split(C_U + 2)
            head_rsqrt(2)
            qk_round(2)
            qk_square(4)
            split(C_U + 3)
            head_rsqrt(3)
            qk_round(3)
            act.wait_ge(v_turned, 1)
            nc.scalar.activation(v_hi[:].rearrange("p b c -> p (b c)"), bank[1][:], ACT.Copy).then_inc(v_hi_done, 1)
            head_rsqrt(4)
            qk_round(4)
            split(C_POOLW)
            d_round(0)
            split(C_WP)
            softmax(0)
            d_round(1)
            split(C_WP + 1)
            softmax(1)
            pr_round(0)
            d_round(2)
            split(C_WP + 2)
            y_round(0)
            softmax(2)
            pool_round(0)
            d_round(3)
            pool_round(1)
            pr_round(1)
            pool_round(2)
            pool_round(3)
            split(C_WP + 3)
            y_round(1)
            act.wait_ge(pool_stat, 1)
            rsqrt(head_rstd[:, 0, :], bank[6][:], G * P, pool_ln, 1, pool_rstd)
            softmax(3)
            split(C_WA)
            pr_round(2)
            split(C_WA + 1)
            y_round(2)
            pr_round(3)
            split(C_WA + 2)
            y_round(3)
            split(C_WA + 3)
            act.wait_ge(y_stat, 1)
            rsqrt(head_rstd[:, 1, :], bank[7][:], NQ * HD, y_ln, 1, y_rstd)
            split(FFN2)
            for d in range(HALF):
                h_round(2, d)
                h_square(2, d)
                if d in (0, 1):
                    split(FFN2 + 1 + d)
            split(FFN2 + 3)
            for d in range(HALF, KD):
                h_round(2, d)
            for d in range(HALF, KD):
                h_square(2, d)
            rstd_of(2, 0)
            ffn_scalar(1, FFN2)
            for d in range(HALF, KD):
                h_square(3, d)

            for half in range(2):
                act.wait_ge(w_used, PROJ + half + 1)
                for b in range(NB):
                    nc.scalar.activation(proj[:, b, half * S:(half + 1) * S], bank[4 * half + b][:],
                                         ACT.Copy).then_inc(proj_kept, 1)
                split(PLE + 2 + half)
            act.wait_ge(ple_stat, 1)
            rsqrt(rstd_nat[:], bank[4][:, 0:2 * NB:2], D, ple_ln, 1, ple_rstd)
            act.wait_ge(ple_rstd, 1)
            for c in range(PLE + SLOTS, PLE + KD):
                split(c)
            for half in range(2):
                for b in range(NB):
                    if b < NB - 1:
                        act.wait_ge(gate_tok, half * (NB - 1) + b + 1)
                    else:
                        act.wait_ge(w_used, PLE + (half + 1) * HALF)
                    if half:
                        act.wait_ge(out_ready, b + 1)
                    nc.scalar.activation(gate[:, b, :], bank[b][:], ACT.Sigmoid,
                                         scale=rstd_nat[:, b:b + 1]).then_inc(gate_ready, 1)

        @block.vector
        def _(dve):
            chained = [0]

            def link(ins):
                chained[0] += 1
                ins.then_inc(dve_chain, 1)
                dve.wait_ge(dve_chain, chained[0])

            def h_rest(ph, d):
                dve.wait_ge(h_hi_done, ph * KD + d + 1)
                nc.vector.scalar_tensor_tensor(h_lo[:, d, :], x_t[:, d, :], gain[:, ph * KD + d:ph * KD + d + 1],
                                               f32(h_hi[:, d, :]), ALU.mult, ALU.subtract).then_inc(h_ready, 1)

            def h_add(ph, d):
                if d == 0:
                    return
                dve.wait_ge(sq_done, ph * KD + d + 1)
                if d > 1:
                    dve.wait_ge(sumsq_added, ph * (KD - 1) + d - 1)
                nc.vector.tensor_tensor(sumsq[:], sumsq[:], tmp[:, 2 + d % 2, :], ALU.add).then_inc(sumsq_added, 1)

            def ffn_vector(n, c0):
                dve.wait_ge(rstd_ready, 2 * n + 1)
                dve.wait_ge(sumsq_added, (2 * n + 1) * (KD - 1))

                def tile(f, quad=0, first=False):
                    count = n * NF + f + 1 + 2 * quad
                    a = tmp[:, 2 * (f % 2), :]
                    t = tmp[:, 2 * (f % 2) + 1, :]
                    gb, ub = (bank[4 * n + 2 * (f % 2) + i] for i in range(2))
                    dve.wait_ge(w_used, c0 + 2 * f + 1 + SLOTS * quad)
                    if not first:
                        dve.wait_ge(act_ready, count - 2)
                    nc.vector.tensor_tensor(a, gb[:], rstd[:], ALU.mult).then_inc(gate_scaled, 1)
                    dve.wait_ge(w_used, c0 + 2 * f + 2 + SLOTS * quad)
                    dve.wait_ge(silu_done, count)
                    nc.vector.tensor_tensor(t, ub[:], a, ALU.mult).then_inc(act_made, 1)
                    dve.wait_ge(act_hi_done, count)
                    nc.vector.tensor_tensor(act_lo[:, f + 2 * quad, :], t, f32(act_hi[:, f + 2 * quad, :]),
                                            ALU.subtract).then_inc(act_ready, 1)

                tile(0, first=True)
                tile(1, first=True)
                with dve.Fori(1, QUADS) as quad:
                    tile(0, quad)
                    tile(1, quad)

                ph = 2 * n + 1
                for half, banks in enumerate(halves(n)):
                    last = c0 + GU + (half + 1) * DH
                    for i in range(HALF):
                        d = half * HALF + i
                        if i < HALF - 1:
                            dve.wait_ge(down_done, (2 * n + half) * (HALF - 1) + i + 1)
                        else:
                            dve.wait_ge(w_used, last)
                        if half == 0 and i == 0:
                            dve.wait_ge(act_ready, (n + 1) * NF)
                        link(nc.vector.scalar_tensor_tensor(tmp[:, i % 2, :], bank[banks[i]][:], 0.5, rstd[:],
                                                            ALU.mult, ALU.mult))
                        nc.vector.tensor_tensor(x_t[:, d, :], x_t[:, d, :], tmp[:, i % 2, :], ALU.add)\
                            .then_inc(x_ready, 1)
                        dve.wait_ge(x_ready, (2 * n + 1) * KD + d + 1)
                    for i in range(HALF):
                        h_rest(ph, half * HALF + i)
                        if half == 0:
                            h_add(ph, i)
                for d in range(HALF, KD):
                    h_add(ph, d)

            nc.vector.memset(ones[:], 1.0).then_inc(dve_consts, 1)
            nc.vector.memset(eps[:], EPS).then_inc(dve_consts, 1)
            link(nc.vector.memset(head_ones[:], 0.0))
            for g in range(2):
                nc.vector.memset(head_ones[g * HD:(g + 1) * HD, g * HD:(g + 1) * HD], 1.0).then_inc(dve_consts, 1)
            for i in range(PAD):
                nc.vector.memset(inv_count[:, i:i + 1], 1.0 / (i + 1)).then_inc(dve_consts, 1)
            dve.wait_ge(dve_consts, 4 + PAD)

            def later_gains():
                dve.wait_ge(gain_turned, 2)
                link(nc.vector.tensor_copy(gain[:, KD:], bank[7][:, KD:GAINS]))
                nc.vector.scalar_tensor_tensor(gain_qk[:], gain[:, GAINS - 2:GAINS - 1], HD ** -0.5, gain[:, GAINS - 1:GAINS], ALU.mult, ALU.mult)\
                    .then_inc(gain_ready, 1)
                nc.vector.tensor_tensor(gain_pool[:], gain[:, 4 * KD:4 * KD + G], gain[:, 4 * KD + G:4 * KD + 2 * G],
                                        ALU.mult).then_inc(gain_ready, 1)
                dve.wait_ge(sinks_loaded, 16)
                nc.vector.tensor_copy(sink[:].rearrange("p (t g) -> p g t", g=2),
                                      sink_in[:].rearrange("p (g t) -> p g t", g=2)).then_inc(gain_ready, 1)
            for pair in range(HALF):
                for d in (2 * pair, 2 * pair + 1):
                    dve.wait_ge(x_turned, d + 1)
                    nc.vector.tensor_copy(x_t[:, d, :], bank[4 + d % 4][:]).then_inc(x_ready, 1)
                dve.wait_ge(x_ready, 2 * pair + 2)
                if pair == 0:
                    dve.wait_ge(gain_turned, 1)
                    nc.vector.tensor_copy(gain[:, 0:KD], bank[7][:, 0:KD]).then_inc(gain1_ready, 1)
                    dve.wait_ge(gain1_ready, 1)
                h_rest(0, 2 * pair)
                h_rest(0, 2 * pair + 1)
                if pair == 1:
                    h_add(0, 1)
                if pair == 2:
                    h_add(0, 2)
                    h_add(0, 3)
            for d in range(HALF, KD):
                h_add(0, d)
            later_gains()
            for k in range(2):
                dve.wait_ge(p_hi_done, k + 1)
                nc.vector.tensor_tensor(pt_lo[:, k, :], bank[5 + k][:], f32(pt_hi[:, k, :]), ALU.subtract)\
                    .then_inc(p_ready, 1)
            ffn_vector(0, FFN1)

            dve.wait_ge(w_used, MIX)
            for t in (kz_hi, kz_lo):
                nc.vector.memset(f32(t[0:HD, 1, :]), 0.0).then_inc(kz_zeroed, 1)
                nc.vector.memset(f32(t[HD:P, 0, :]), 0.0).then_inc(kz_zeroed, 1)
            link(nc.vector.memset(win[:, :, 0:PAD], 0.0))
            dve.wait_ge(rstd_ready, 2)

            def qk_scale(i):
                if i < 4:
                    dve.wait_ge(w_used, C_K + i + 1)
                    src = bank[4 + i]
                else:
                    dve.wait_ge(w_used, C_Q3 + 1)
                    src = bank[2]
                nc.vector.tensor_tensor(qk[i], src[:], rstd[:], ALU.mult).then_inc(qk_scaled, 1)

            def qk_norm(i):
                dve.wait_ge(head_rstd_ready, i + 1)
                dve.wait_ge(qk_scaled, i + 1)
                r = head_rstd[:, i % 2, :]
                if i == 0:
                    nc.vector.scalar_tensor_tensor(qk[0], qk[0], gain_qk[:, 0:1], r, ALU.mult, ALU.mult)\
                        .then_inc(qk_normed, 1)
                    dve.wait_ge(qk_hi_done, 2)
                    dve.wait_ge(kz_zeroed, 4)
                    for g in range(2):
                        rows = slice(g * HD, (g + 1) * HD)
                        nc.vector.tensor_tensor(kz_lo[rows, g, :], qk[0][rows], f32(kz_hi[rows, g, :]), ALU.subtract)\
                            .then_inc(qk_ready, 1)
                else:
                    nc.vector.tensor_tensor(qk[i], qk[i], r, ALU.mult).then_inc(qk_normed, 1)
                    dve.wait_ge(qk_hi_done, 2 + i)
                    nc.vector.tensor_tensor(q_lo[:, i - 1, :], qk[i], f32(q_hi[:, i - 1, :]), ALU.subtract)\
                        .then_inc(qk_ready, 1)

            def u_scale(g):
                dve.wait_ge(w_used, C_U + g + 1)
                nc.vector.tensor_tensor(win[:, 0, PAD:], bank[4 + g][:], rstd[:], ALU.mult).then_inc(u_scaled, 1)

            def d_make(g):
                w = POOL_WINDOWS[g]
                u, total = win[:, 0, :], win[:, 1 + g % 2, :]
                dve.wait_ge(win_summed, g + 1)
                d = head_rstd[:, 1, :]
                if g:
                    dve.wait_ge(d_ready, g)
                link(nc.vector.scalar_tensor_tensor(d, total[:, PAD:], 1.0 / w, u[:, PAD:], ALU.mult, ALU.subtract))
                head = total[:, PAD:PAD + w]
                link(nc.vector.tensor_tensor(head, head, inv_count[:, 0:w], ALU.mult))
                nc.vector.tensor_tensor(d[:, 0:w], head, u[:, PAD:PAD + w], ALU.subtract).then_inc(d_made, 1)

            def d_rest(g):
                dve.wait_ge(d_hi_done, g + 1)
                dve.wait_ge(d_made, g + 1)
                nc.vector.tensor_tensor(d_lo[:, g, :], head_rstd[:, 1, :], f32(d_hi[:, g, :]), ALU.subtract)\
                    .then_inc(d_ready, 1)

            def row_max(b):
                if b == 0:
                    dve.wait_ge(qk_ready, 6)
                elif b > 1:
                    dve.wait_ge(p_normed, b - 1)
                sm = small[:, b % 2]
                lo = P if b == 0 else 0
                for n in range(NQ):
                    if n % 2 == 0:
                        dve.wait_ge(s_done, QP * b + n // 2 + 1)
                    nc.vector.tensor_tensor_reduce(
                        out=probs[:, b % 2, n, lo:], in0=bank[n // 2][:, (n % 2) * 2 * P + lo:(n % 2 + 1) * 2 * P],
                        in1=mask[:].rearrange("p a k -> p (a k)")[:, lo:], scale=1.0, scalar=-3.0e38,
                        op0=ALU.add, op1=ALU.max, accum_out=sm[:, 0, n:n + 1]).then_inc(s_taken, 1)
                dve.wait_ge(s_taken, NQ * (b + 1))
                link(nc.vector.tensor_tensor(sm[:, 5, :], sm[:, 0, :], sink[:], ALU.max))
                link(nc.vector.tensor_scalar(sm[:, 1, :], sm[:, 5, :], -1.0, None, ALU.mult))
                nc.vector.tensor_tensor(sm[:, 2, :], sink[:], sm[:, 5, :], ALU.subtract).then_inc(max_ready, 1)

            def normalise(b):
                lo = P if b == 0 else 0
                dve.wait_ge(exp_done, (NQ + 1) * (b + 1))
                sm = small[:, b % 2]
                link(nc.vector.tensor_tensor(sm[:, 6, :], sm[:, 4, :], sm[:, 3, :], ALU.add))
                link(nc.vector.reciprocal(sm[:, 7, :], sm[:, 6, :]))
                pb = probs[:, b % 2, :, lo:]
                nc.vector.tensor_tensor(pb, pb, sm[:, 7, :].unsqueeze(2).broadcast_to([P, NQ, 2 * P - lo]),
                                        ALU.mult).then_inc(p_normed, 1)

            def pr_rest(b):
                base = 0 if b == 0 else 4 * b - 2
                for i, slot in enumerate((1, 3) if b == 0 else range(4)):
                    dve.wait_ge(pr_hi_done, base + i + 1)
                    nc.vector.tensor_tensor(pr_lo[:, slot, :], bank[slot][:], f32(pr_hi[:, slot, :]), ALU.subtract)\
                        .then_inc(pr_ready, 1)

            def y_rest(b):
                if b:
                    dve.wait_ge(y_ready, b)
                for g in range(2):
                    rows = slice(g * HD, (g + 1) * HD)
                    dve.wait_ge(pv_done, 2 * b + g + 1)
                    nc.vector.tensor_tensor(
                        tmp[rows, 1, :].rearrange("p (t q) -> p t q", t=QP),
                        bank[4 + g][rows].rearrange("p (t q) -> p t q", t=QP),
                        gain[rows, 5 * KD:5 * KD + QP].unsqueeze(2).broadcast_to([HD, QP, P]), ALU.mult)\
                        .then_inc(y_made, 1)
                dve.wait_ge(y_hi_done, b + 1)
                dve.wait_ge(y_made, 2 * b + 2)
                nc.vector.tensor_tensor(h_lo[:, G:, b * P:(b + 1) * P], tmp[:, 1, :].rearrange("p (t q) -> p t q", t=QP),
                                        f32(h_hi[:, G:, b * P:(b + 1) * P]), ALU.subtract).then_inc(y_ready, 1)
                dve.wait_ge(y_sq_done, 2 * b + 2)
                nc.vector.tensor_reduce(tmp[:, 3, b * P:(b + 1) * P], tmp[:, 2, :].rearrange("p (t q) -> p q t", t=QP),
                                        mybir.AxisListType.X, ALU.add).then_inc(y_summed, 1)

            def wp_add(d):
                if d % 2 == 0:
                    dve.wait_ge(wp_even, d // 2 + 1)
                else:
                    dve.wait_ge(w_used, C_WP + d // 2 + 1)
                dve.wait_ge(pool_rstd, 1)
                if d:
                    dve.wait_ge(wp_added, d)
                link(nc.vector.tensor_tensor(tmp[:, 0, :], bank[6 + (d + 1) % 2][:], head_rstd[:, 0, :], ALU.mult))
                nc.vector.tensor_tensor(x_t[:, d, :], x_t[:, d, :], tmp[:, 0, :], ALU.add).then_inc(wp_added, 1)

            def pool_rest(g):
                dve.wait_ge(pool_sq_done, g + 1)
                nc.vector.scalar_tensor_tensor(h_lo[:, g, :], bank[6 + g % 2][:], gain_pool[:, g:g + 1],
                                               f32(h_hi[:, g, :]), ALU.mult, ALU.subtract).then_inc(pool_ready, 1)
                if g:
                    if g > 1:
                        dve.wait_ge(pool_summed, g - 1)
                    nc.vector.tensor_tensor(sumsq[:], sumsq[:], rstd[:], ALU.add).then_inc(pool_summed, 1)

            for i in range(4):
                qk_scale(i)
            qk_norm(0)
            dve.wait_ge(w_used, C_V + 1)
            nc.vector.tensor_tensor(tmp[:, 0, :], bank[1][:], rstd[:], ALU.mult).then_inc(v_scaled, 1)
            qk_norm(1)
            qk_norm(2)
            qk_scale(4)
            qk_norm(3)
            u_scale(0)
            dve.wait_ge(v_hi_done, 1)
            nc.vector.tensor_tensor(v_lo[:].rearrange("p b c -> p (b c)"), bank[1][:],
                                    f32(v_hi[:].rearrange("p b c -> p (b c)")), ALU.subtract).then_inc(v_ready, 1)
            qk_norm(4)
            d_make(0)
            d_rest(0)
            u_scale(1)
            row_max(0)
            d_make(1)
            normalise(0)
            d_rest(1)
            u_scale(2)
            row_max(1)
            d_make(2)
            pr_rest(0)
            normalise(1)
            d_rest(2)
            u_scale(3)
            y_rest(0)
            row_max(2)
            pool_rest(0)
            d_make(3)
            d_rest(3)
            pool_rest(1)
            pr_rest(1)
            normalise(2)
            pool_rest(2)
            pool_rest(3)
            y_rest(1)
            row_max(3)
            wp_add(0)
            normalise(3)
            wp_add(1)
            pr_rest(2)
            wp_add(2)
            y_rest(2)
            wp_add(3)
            pr_rest(3)
            wp_add(4)
            wp_add(5)
            y_rest(3)
            wp_add(6)
            wp_add(7)
            for d in range(KD):
                if d % 2 == 0:
                    dve.wait_ge(wa_even, d // 2 + 1)
                else:
                    dve.wait_ge(w_used, C_WA + d // 2 + 1)
                dve.wait_ge(y_rstd, 1)
                dve.wait_ge(wp_added, KD)
                link(nc.vector.tensor_tensor(tmp[:, d % 2, :], bank[d % 4][:], head_rstd[:, 1, :], ALU.mult))
                nc.vector.tensor_tensor(x_t[:, d, :], x_t[:, d, :], tmp[:, d % 2, :], ALU.add).then_inc(x_ready, 1)
                dve.wait_ge(x_ready, 2 * KD + d + 1)
                if 1 <= d <= HALF:
                    h_rest(2, d - 1)
                    h_add(2, d - 1)
            for d in range(HALF, KD):
                h_rest(2, d)
            for d in range(HALF, KD):
                h_add(2, d)
            ffn_vector(1, FFN2)

            for half in range(2):
                for b in range(NB):
                    dve.wait_ge(gate_ready, half * NB + b + 1)
                    dve.wait_ge(proj_kept, 2 * NB)
                    o = proj[:, b, half * S:(half + 1) * S]
                    link(nc.vector.tensor_tensor(o, o, gate[:, b, :], ALU.mult))
                    dve.wait_ge(x_back, half * NB + b + 1)
                    nc.vector.tensor_tensor(o, o, bank[4 + b][:], ALU.add).then_inc(out_ready, 1)

        @block.tensor
        def _(pe):
            def product(dst, a_hi, a_lo, b_hi, b_lo, first, last):
                nc.tensor.matmul(dst, a_hi, b_hi, start=first, stop=False)
                nc.tensor.matmul(dst, a_hi, b_lo, start=False, stop=False)
                return nc.tensor.matmul(dst, a_lo, b_hi, start=False, stop=last)

            def from_chunk(dst, slot, col, b_hi, b_lo, first, last):
                return product(dst, w_hi[:, slot, col:col + P], w_lo[:, slot, col:col + P], b_hi, b_lo, first, last)

            def from_h(dst, slot, k_from, k_to):
                for k in range(k_from, k_to):
                    ins = from_chunk(dst, slot, k * P, h_hi[:, k, :], h_lo[:, k, :], k == 0, k == KD - 1)
                return ins

            def turn(dst, src, rows=P):
                return nc.tensor.transpose(dst, src, ident[0:rows, 0:rows])

            def stat(ph, b):
                pe.wait_ge(sumsq_added, (ph + 1) * (KD - 1))
                nc.tensor.matmul(bank[b][:], ones[:], sumsq[:], start=True, stop=True).then_inc(stat_done, 1)

            def opening(ph, c0, banks, stat_bank):
                for lower in (True, False):
                    for j in range(SLOTS):
                        slot = (c0 + j) % SLOTS
                        if lower:
                            pe.wait_ge(w_ready, c0 + j + 1)
                        for k in range(0 if lower else HALF, HALF if lower else KD):
                            if j == 0:
                                pe.wait_ge(h_ready, ph * KD + k + 1)
                            ins = from_h(bank[banks[j]][:], slot, k, k + 1)
                        if not lower:
                            ins.then_inc(w_used, 1)
                            if j == 0:
                                stat(ph, stat_bank)

            def ffn_tensor(n, c0):
                gu = [4 * n + i for i in range(4)]
                with pe.Fori(1, QUADS) as quad:
                    for j in range(SLOTS):
                        slot = (c0 + j) % SLOTS
                        pe.wait_ge(w_ready, quad * SLOTS + c0 + j + 1)
                        pe.wait_ge((gate_scaled, act_made)[j % 2], quad * 2 + n * NF + j // 2 - 1)
                        from_h(bank[gu[j]][:], slot, 0, KD).then_inc(w_used, 1)
                for half, banks in enumerate(halves(n)):
                    first = c0 + GU + half * DH
                    if half == 0:
                        pe.wait_ge(act_ready, (n + 1) * NF - 2)
                        if n == 0:
                            pe.wait_ge(p_ready, 2)
                        else:
                            pe.wait_ge(x_ready, 3 * KD)
                    else:
                        pe.wait_ge(act_made, (n + 1) * NF)

                    def step(ch, slot, quad):
                        q = 0 if quad is None else quad
                        pe.wait_ge(w_ready, q * SLOTS + first + ch + 1)
                        if ch == DH - 1:
                            pe.wait_ge(act_ready, (n + 1) * NF)
                        last = ch == DH - 1
                        order = [(kk, i) for kk in range(2) for i in range(HALF)]
                        if last:
                            order = [(kk, i) for i in range(HALF) for kk in range(2)]
                        for kk, i in order:
                            k = q * 2 * SLOTS + 2 * ch + kk
                            ins = from_chunk(bank[banks[i]][:], slot, (kk * HALF + i) * P, act_hi[:, k, :],
                                             act_lo[:, k, :], ch == 0 and kk == 0, last and kk == 1)
                            if last and kk == 1 and i < HALF - 1:
                                ins.then_inc(down_done, 1)
                        ins.then_inc(w_used, 1)

                    down_steps(pe, first, step)

            pe.wait_ge(ident_ready, 1)
            def turn_x(d):
                if d % 2 == 0:
                    pe.wait_ge(x_loaded[d // 2], 16)
                if d == 3:
                    pe.wait_ge(gain1_ready, 1)
                if d >= 4:
                    pe.wait_ge(x_ready, d - 3)
                for b in range(NB):
                    ins = turn(bank[4 + d % 4][:, b * P:(b + 1) * P], x_nat[:, b, d * P:(d + 1) * P])
                ins.then_inc(x_turned, 1)

            turn_x(0)
            turn_x(1)
            pe.wait_ge(gain1_loaded, 16)
            turn(bank[7][:, 0:KD], gain_nat[0:KD, :], KD).then_inc(gain_turned, 1)
            turn_x(2)
            turn_x(3)
            for pair in range(HALF):
                pe.wait_ge(h_ready, 2 * pair + 2)
                for j in range(2):
                    if pair == 0:
                        pe.wait_ge(w_ready, j + 1)
                    ins = from_h(bank[j][:], j, 2 * pair, 2 * pair + 2)
                    if pair == HALF - 1:
                        ins.then_inc(w_used, 1)
                if pair < 2:
                    turn_x(4 + 2 * pair)
                    turn_x(5 + 2 * pair)
            pe.wait_ge(gains_loaded, 16 * 11)
            pe.wait_ge(x_ready, KD)
            turn(bank[7][:, 0:GAINS], gain_nat[:], GAINS).then_inc(gain_turned, 1)
            pe.wait_ge(p_loaded, 16)
            for k in range(2):
                for b in range(NB):
                    ins = turn(bank[5 + k][:, b * P:(b + 1) * P], p_nat[:, b, k * P:(k + 1) * P])
                ins.then_inc(p_turned, 1)
            for j in range(2, SLOTS):
                pe.wait_ge(w_ready, j + 1)
                from_h(bank[j][:], j, 0, HALF)
                if j == 2:
                    pe.wait_ge(dve_consts, 4 + PAD)
                    stat(0, 4)
                from_h(bank[j][:], j, HALF, KD).then_inc(w_used, 1)
            ffn_tensor(0, FFN1)

            pe.wait_ge(x_ready, KD + HALF)
            opening(1, MIX, [4, 5, 6, 7], 0)

            def in_chunk(c, b):
                pe.wait_ge(w_ready, c + 1)
                from_h(bank[b][:], c % SLOTS, 0, KD).then_inc(w_used, 1)

            def head_ms(i):
                pe.wait_ge(qk_sq_done, i + 1)
                if i >= 2:
                    pe.wait_ge(head_ln_done, i - 1)
                else:
                    pe.wait_ge(rstd_ready, 2)
                nc.tensor.matmul(bank[(0, 3)[i % 2]][:], head_ones[:], qk_sq[i % 3], start=True, stop=True)\
                    .then_inc(head_ms_done, 1)

            def scores(b):
                pe.wait_ge(qk_ready, 6)
                if b == 0:
                    pe.wait_ge(head_ln_done, 1 + QP)
                    pe.wait_ge(v_ready, 1)
                for t in range(QP):
                    if b:
                        pe.wait_ge(s_taken, NQ * (b - 1) + 2 * t + 2)
                        if b > 1:
                            pe.wait_ge(pr_ready, 4 * (b - 1) - 2)
                    lo, width = (P, P) if b == 0 else (0, 2 * P)
                    key = max(b - 1, 0) * P
                    q = slice(b * P, (b + 1) * P)
                    dst = bank[t][:].rearrange("p (g k) -> p g k", g=2)[:, :, lo:]
                    product(dst, q_hi[:, t, q], q_lo[:, t, q], kz_hi[:, :, key:key + width],
                            kz_lo[:, :, key:key + width], True, True).then_inc(s_done, 1)

            def turn_probs(b):
                pe.wait_ge(p_normed, b + 1)
                pe.wait_ge(s_taken, NQ * min(b + 2, NB))
                for g in range(2):
                    for kb in range(1 if b == 0 else 0, 2):
                        for t in range(QP):
                            ins = turn(bank[2 * g + kb][:, t * P:(t + 1) * P],
                                       probs[:, b % 2, 2 * t + g, kb * P:(kb + 1) * P])
                        ins.then_inc(pr_turned, 1)

            def values(b):
                if b:
                    pe.wait_ge(y_sq_done, 2 * b)
                    pe.wait_ge(y_made, 2 * b)
                else:
                    pe.wait_ge(u_scaled, 2)
                base = 0 if b == 0 else 4 * b - 2
                kbs = range(1 if b == 0 else 0, 2)
                for g in range(2):
                    pe.wait_ge(pr_ready, base + (g + 1) * len(kbs))
                    for kb in kbs:
                        ins = product(bank[4 + g][:], v_hi[:, b - 1 + kb, :], v_lo[:, b - 1 + kb, :],
                                      pr_hi[:, 2 * g + kb, :], pr_lo[:, 2 * g + kb, :], kb == kbs[0], kb == 1)
                    ins.then_inc(pv_done, 1)

            def wp(d):
                c = C_WP + d // 2
                pe.wait_ge(w_ready, c + 1)
                if d >= 2:
                    pe.wait_ge(wp_added, d - 1)
                elif d == 1:
                    pe.wait_ge(pool_rstd, 1)
                else:
                    pe.wait_ge(pool_ready, G)
                for k in range(G):
                    ins = from_chunk(bank[6 + (d + 1) % 2][:], c % SLOTS, (2 * k + d % 2) * P, h_hi[:, k, :], h_lo[:, k, :],
                                     k == 0, k == G - 1)
                ins.then_inc((wp_even, w_used)[d % 2], 1)

            def pool_map(g):
                pe.wait_ge(w_ready, C_POOLW + 1)
                pe.wait_ge(d_ready, g + 1)
                pe.wait_ge(u_scaled, 3 + g) if g < 2 else pe.wait_ge(pool_ready, g - 1)
                from_chunk(bank[6 + g % 2][:], C_POOLW % SLOTS, g * P, d_hi[:, g, :], d_lo[:, g, :], True, True)\
                    .then_inc(pool_done if g < G - 1 else w_used, 1)

            head_ms(0)
            in_chunk(C_V, 1)
            head_ms(1)
            head_ms(2)
            in_chunk(C_Q3, 2)
            head_ms(3)
            pe.wait_ge(qk_scaled, 1)
            in_chunk(C_U, 4)
            pe.wait_ge(v_scaled, 1)
            for b in range(NB):
                ins = turn(bank[1][:, b * P:(b + 1) * P], tmp[:, 0, b * P:(b + 1) * P])
            ins.then_inc(v_turned, 1)
            head_ms(4)
            pe.wait_ge(qk_scaled, 2)
            in_chunk(C_U + 1, 5)
            scores(0)
            pe.wait_ge(qk_scaled, 3)
            in_chunk(C_U + 2, 6)
            scores(1)
            turn_probs(0)
            pe.wait_ge(qk_scaled, 4)
            in_chunk(C_U + 3, 7)
            values(0)
            scores(2)
            pool_map(0)
            pool_map(1)
            turn_probs(1)
            pool_map(2)
            pool_map(3)
            values(1)
            scores(3)
            pe.wait_ge(pool_summed, G - 1)
            pe.wait_ge(pool_ready, G - 1)
            nc.tensor.matmul(bank[6][:], ones[:], sumsq[:], start=True, stop=True).then_inc(pool_stat, 1)
            wp(0)
            wp(1)
            turn_probs(2)
            wp(2)
            values(2)
            wp(3)
            turn_probs(3)
            wp(4)
            wp(5)
            values(3)
            wp(6)
            wp(7)
            for d in range(KD):
                c = C_WA + d // 2
                if d == 0:
                    pe.wait_ge(y_ready, NB)
                pe.wait_ge(w_ready, c + 1)
                if d >= 4:
                    pe.wait_ge(x_ready, 2 * KD + d - 3)
                for k in range(QP):
                    ins = from_chunk(bank[d % 4][:], c % SLOTS, (2 * k + d % 2) * P, h_hi[:, G + k, :],
                                     h_lo[:, G + k, :], k == 0, k == QP - 1)
                ins.then_inc((wa_even, w_used)[d % 2], 1)
                if d == 1:
                    pe.wait_ge(y_summed, NB)
                    pe.wait_ge(wp_added, KD)
                    nc.tensor.matmul(bank[7][:], ones[:], tmp[:, 3, :], start=True, stop=True).then_inc(y_stat, 1)

            pe.wait_ge(y_rstd, 1)
            opening(2, FFN2, [4, 5, 6, 7], 0)
            ffn_tensor(1, FFN2)

            for half in range(2):
                pe.wait_ge(x_ready, 3 * KD + (half + 1) * HALF)
                pe.wait_ge(w_ready, PROJ + half + 1)
                slot = (PROJ + half) % SLOTS
                for b in range(NB):
                    tok = slice(b * P, (b + 1) * P)
                    for k in range(2):
                        ins = product(bank[4 * half + b][:], pt_hi[:, k, tok], pt_lo[:, k, tok],
                                      w_hi[:, slot, k * S:(k + 1) * S], w_lo[:, slot, k * S:(k + 1) * S],
                                      k == 0, k == 1)
                ins.then_inc(w_used, 1)

            def ple_chunk(half, i):
                c = PLE + half * HALF + i
                slot = c % SLOTS
                pe.wait_ge(w_ready, c + 1)
                for b in range(NB):
                    if i == 0:
                        if half:
                            pe.wait_ge(gate_ready, b + 1)
                        else:
                            pe.wait_ge(proj_kept, b + 1)
                    tok = slice(b * P, (b + 1) * P)
                    for kk in range(2):
                        k = 2 * i + kk
                        pe.wait_ge(h_ready, 3 * KD + k + 1) if b == 0 and half == 0 else None
                        ins = product(bank[b][:], h_hi[:, k, tok], h_lo[:, k, tok],
                                      w_hi[:, slot, kk * S:(kk + 1) * S], w_lo[:, slot, kk * S:(kk + 1) * S],
                                      k == 0, k == KD - 1)
                    if i == HALF - 1 and b < NB - 1:
                        ins.then_inc(gate_tok, 1)
                ins.then_inc(w_used, 1)

            def x_to_tokens(half):
                for b in range(NB):
                    if half:
                        pe.wait_ge(out_ready, b + 1)
                    for d in range(HALF):
                        ins = turn(bank[4 + b][:, d * P:(d + 1) * P], x_t[:, half * HALF + d, b * P:(b + 1) * P])
                    ins.then_inc(x_back, 1)

            for i in range(HALF):
                ple_chunk(0, i)
                if i == 1:
                    pe.wait_ge(sumsq_added, 4 * (KD - 1))
                    pe.wait_ge(proj_kept, 2 * NB)
                    for b in range(NB):
                        ins = nc.tensor.matmul(bank[4][:, 2 * b:2 * b + 2], sumsq[:, b * P:(b + 1) * P], ones[:, 0:2],
                                               start=True, stop=True)
                    ins.then_inc(ple_stat, 1)
                if i == 2:
                    pe.wait_ge(ple_rstd, 1)
                    x_to_tokens(0)
            for i in range(HALF):
                ple_chunk(1, i)
                if i == 1:
                    x_to_tokens(1)


_INPUTS = ["x", "p", "ffn1_norm", "ffn1_w_gate", "ffn1_w_up", "ffn1_w_down", "mix_norm", "w_in", "pool_w",
           "pool_scale", "q_norm", "k_norm", "attn_sinks", "pool_out_norm", "attn_out_norm", "w_out", "ffn2_norm",
           "ffn2_w_gate", "ffn2_w_up", "ffn2_w_down", "ple_norm", "w_ple_gate", "w_ple_proj"]


def kernel(**inputs):
    import numpy as np
    import concourse.bacc as bacc
    from concourse.bass_utils import run_bass_kernel_spmd

    nc = bacc.Bacc("TRN2", target_bir_lowering=False, num_devices=1)
    arrays, args = {}, []
    for name in _INPUTS:
        a = np.ascontiguousarray(inputs[name])
        arrays["in_" + name] = a
        args.append(nc.dram_tensor("in_" + name, a.shape, mybir.dt.from_np(a.dtype), kind="ExternalInput").ap())
    shape = arrays["in_x"].shape
    args.append(nc.dram_tensor("out_x", shape, F32, kind="ExternalOutput").ap())
    layer(nc, *args)
    r = run_bass_kernel_spmd(nc, [arrays], core_ids=[0])
    return r.results[0]["out_x"]
```
